# Optimizing a Trainium2 kernel written in Bass

```python
import math
import jax
import jax.numpy as jnp
from jax import lax
import numpy as np

D_MODEL = 2048
BATCH = 1
SEQ = 512
DEPTH = 1

MIX_W = D_MODEL
POOL_W = MIX_W // 4
POOL_WINDOWS = (2, 4, 8, 16)
POOL_GROUP = POOL_W // len(POOL_WINDOWS)
GLA_W = MIX_W // 4
GLA_HEADS = 4
GLA_DV = GLA_W // GLA_HEADS
GLA_DK = GLA_DV // 2
GLA_RANK = 16
GLA_GATE_NORM = 16.0
GLA_CHUNK = 64
NSA_W = MIX_W // 2
NSA_HEAD_DIM = 64
NSA_HEADS = NSA_W // NSA_HEAD_DIM
NSA_GROUPS = 4
NSA_KV_W = NSA_GROUPS * NSA_HEAD_DIM
CMP_BLOCK = 32
CMP_STRIDE = 16
CMP_HIDDEN = 256
SLC_BLOCK = 64
N_SELECT = 16
WINDOW = 512
NSA_QBLOCK = 32
FORCE_BONUS = 100.0
FFN_HIDDEN = -(-8 * D_MODEL // (3 * 256)) * 256
EPS = 1e-6

IN_SIZES = (
    POOL_W,
    GLA_HEADS * GLA_DK,
    GLA_HEADS * GLA_DK,
    GLA_W,
    GLA_W,
    GLA_RANK,
    NSA_W,
    NSA_KV_W, NSA_KV_W,
    NSA_KV_W, NSA_KV_W,
    NSA_KV_W, NSA_KV_W,
    NSA_HEADS * 3,
)
IN_W = sum(IN_SIZES)

kernel_name = 'hybrid_pool_gla_nsa_block'

def rms_norm(x, gain):
    xf = x.astype(jnp.float32)
    y = xf * lax.rsqrt(jnp.mean(xf * xf, axis=-1, keepdims=True) + EPS)
    return y.astype(x.dtype) * gain

def modulate(h, shift, scale):
    return h * (1.0 + scale[:, None, :]) + shift[:, None, :]

def masked_softmax(s, mask):
    s = jnp.where(mask, s.astype(jnp.float32), -jnp.inf)
    m = jnp.max(s, axis=-1, keepdims=True)
    m = jnp.where(jnp.isfinite(m), m, 0.0)
    e = jnp.exp(s - m)
    d = jnp.sum(e, axis=-1, keepdims=True)
    return e / jnp.where(d > 0, d, 1.0)

def alibi_slopes(n):
    return np.asarray([2.0 ** (-8.0 * (i + 1) / n) for i in range(n)], dtype=np.float32)

def pool_mixer(u, w_pool, scale):
    b, s, _ = u.shape
    ng = len(POOL_WINDOWS)
    ug = u.reshape(b, s, ng, POOL_GROUP)
    cs = jnp.cumsum(ug.astype(jnp.float32), axis=1)
    cs = jnp.concatenate([jnp.zeros_like(cs[:, :1]), cs], axis=1)
    t = jnp.arange(s)
    pooled = []
    for gi, w in enumerate(POOL_WINDOWS):
        lo = jnp.maximum(t + 1 - w, 0)
        win_sum = cs[:, 1:, gi] - cs[:, lo, gi]
        pooled.append(win_sum / (t + 1 - lo).astype(jnp.float32)[None, :, None])
    pooled = jnp.stack(pooled, axis=2)
    d = (pooled - ug.astype(jnp.float32)).astype(u.dtype)
    y = jnp.einsum('bsgc,gce->bsge', d, w_pool)
    return y.reshape(b, s, POOL_W) * scale

def gla_chunked(q, k, v, log_a):
    b, s, h, dk = q.shape
    dv = v.shape[-1]
    n = s // GLA_CHUNK

    def chunks(a):
        return jnp.moveaxis(a.astype(jnp.float32).reshape(b, n, GLA_CHUNK, h, a.shape[-1]), 1, 0)

    qc, kc, vc = chunks(q), chunks(k), chunks(v)
    bc = jnp.cumsum(chunks(log_a), axis=2)
    causal = jnp.tril(jnp.ones((GLA_CHUNK, GLA_CHUNK), dtype=bool))[None, :, :, None, None]

    def step(state, inp):
        qi, ki, vi, bi = inp
        inter = jnp.einsum('bchd,bhde->bche', qi * jnp.exp(bi), state)
        dec = jnp.exp(jnp.where(causal, bi[:, :, None] - bi[:, None, :], -jnp.inf))
        att = jnp.einsum('bihd,bjhd,bijhd->bhij', qi, ki, dec)
        intra = jnp.einsum('bhij,bjhe->bihe', att, vi)
        last = bi[:, -1]
        state = (jnp.exp(last)[..., None] * state
                 + jnp.einsum('bchd,bche->bhde', ki * jnp.exp(last[:, None] - bi), vi))
        return state, inter + intra

    state0 = jnp.zeros((b, h, dk, dv), jnp.float32)
    _, out = lax.scan(step, state0, (qc, kc, vc, bc))
    return jnp.moveaxis(out, 0, 1).reshape(b, s, h, dv).astype(v.dtype)

def nsa_attention(q, k_cmp_tok, v_cmp_tok, k_slc, v_slc, k_win, v_win, gates,
                  cmp_pos, cmp_w1, cmp_w2, k_cmp_gain):
    b, s, h, dk = q.shape
    g = NSA_GROUPS
    r = h // g
    slopes = jnp.asarray(alibi_slopes(h).reshape(g, r))

    n_cmp = (s - CMP_BLOCK) // CMP_STRIDE + 1
    cmp_start = np.arange(n_cmp) * CMP_STRIDE
    cmp_idx = cmp_start[:, None] + np.arange(CMP_BLOCK)[None, :]
    cmp_end = jnp.asarray(cmp_idx[:, -1])

    def compress(tok, pos, w1, w2):
        blk = tok[:, cmp_idx] + pos[:, None, :]
        flat = jnp.moveaxis(blk, 3, 2).reshape(b, n_cmp, g, CMP_BLOCK * dk)
        return jax.nn.silu(flat @ w1) @ w2

    k_cmp = rms_norm(compress(k_cmp_tok, cmp_pos[0], cmp_w1[0], cmp_w2[0]), k_cmp_gain)
    v_cmp = compress(v_cmp_tok, cmp_pos[1], cmp_w1[1], cmp_w2[1])

    n_slc = s // SLC_BLOCK
    n_pick = min(N_SELECT, n_slc)
    slc_start = np.arange(n_slc) * SLC_BLOCK
    overlap = np.clip(np.minimum(cmp_start[:, None] + CMP_BLOCK, slc_start[None, :] + SLC_BLOCK)
                      - np.maximum(cmp_start[:, None], slc_start[None, :]), 0, None)
    cmp_to_slc = jnp.asarray((overlap / CMP_STRIDE).astype(np.float32))
    ks_blocks = jnp.moveaxis(k_slc.reshape(b, n_slc, SLC_BLOCK, g, dk), 3, 1)
    vs_blocks = jnp.moveaxis(v_slc.reshape(b, n_slc, SLC_BLOCK, g, dk), 3, 1)
    blk_ids = jnp.arange(n_slc)
    gather_blocks = jax.vmap(jax.vmap(lambda blocks, ix: blocks[ix]))

    pad = ((0, 0), (WINDOW, 0), (0, 0), (0, 0))
    kw_pad = jnp.pad(k_win, pad)
    vw_pad = jnp.pad(v_win, pad)

    qg = q.reshape(b, s, g, r, dk)
    gg = gates.reshape(b, s, g, r, 3)
    nq = s // NSA_QBLOCK

    def block_fn(i):
        q0 = i * NSA_QBLOCK
        qb = lax.dynamic_slice_in_dim(qg, q0, NSA_QBLOCK, axis=1)
        gb = lax.dynamic_slice_in_dim(gg, q0, NSA_QBLOCK, axis=1)
        t = q0 + jnp.arange(NSA_QBLOCK)

        s_c = jnp.einsum('bqgrd,bngd->bgrqn', qb, k_cmp).astype(jnp.float32)
        dist_c = (t[:, None] - cmp_end[None, :]).astype(jnp.float32)
        p_c = masked_softmax(s_c - slopes[:, :, None, None] * dist_c, dist_c >= 0)
        o_c = jnp.einsum('bgrqn,bngd->bqgrd', p_c.astype(v_cmp.dtype), v_cmp)

        imp = jnp.einsum('bgrqn,nj->bgqj', p_c, cmp_to_slc)
        cur = t // SLC_BLOCK
        forced = ((blk_ids[None, :] == 0) | (blk_ids[None, :] == cur[:, None])
                  | (blk_ids[None, :] == cur[:, None] - 1))
        valid_blk = blk_ids[None, :] * SLC_BLOCK <= t[:, None]
        score = jnp.where(valid_blk, imp + FORCE_BONUS * forced.astype(jnp.float32), -jnp.inf)
        _, sel = lax.top_k(score, n_pick)
        gk = gather_blocks(ks_blocks, sel)
        gv = gather_blocks(vs_blocks, sel)
        nl = n_pick * SLC_BLOCK
        s_s = jnp.einsum('bqgrd,bgqnld->bgrqnl', qb, gk).reshape(b, g, r, NSA_QBLOCK, nl)
        pos_s = (sel[..., None] * SLC_BLOCK + jnp.arange(SLC_BLOCK)).reshape(b, g, NSA_QBLOCK, nl)
        dist_s = (t[None, None, :, None] - pos_s).astype(jnp.float32)[:, :, None]
        p_s = masked_softmax(s_s.astype(jnp.float32) - slopes[None, :, :, None, None] * dist_s,
                             dist_s >= 0)
        o_s = jnp.einsum('bgrqk,bgqkd->bqgrd', p_s.astype(gv.dtype),
                         gv.reshape(b, g, NSA_QBLOCK, nl, dk))

        kwb = lax.dynamic_slice_in_dim(kw_pad, q0, WINDOW + NSA_QBLOCK, axis=1)
        vwb = lax.dynamic_slice_in_dim(vw_pad, q0, WINDOW + NSA_QBLOCK, axis=1)
        s_pos = q0 - WINDOW + jnp.arange(WINDOW + NSA_QBLOCK)
        dist_w = t[:, None] - s_pos[None, :]
        valid_w = (dist_w >= 0) & (dist_w < WINDOW) & (s_pos[None, :] >= 0)
        s_w = jnp.einsum('bqgrd,bkgd->bgrqk', qb, kwb).astype(jnp.float32)
        p_w = masked_softmax(s_w - slopes[:, :, None, None] * dist_w.astype(jnp.float32), valid_w)
        o_w = jnp.einsum('bgrqk,bkgd->bqgrd', p_w.astype(vwb.dtype), vwb)

        o = gb[..., 0:1] * o_c + gb[..., 1:2] * o_s + gb[..., 2:3] * o_w
        return o.reshape(b, NSA_QBLOCK, h * dk)

    outs = lax.map(block_fn, jnp.arange(nq))
    return jnp.moveaxis(outs, 0, 1).reshape(b, s, h * dk)

def setup_inputs(seed: int = 0) -> dict:
    key = jax.random.key(seed)
    ks = jax.random.split(key, 20)
    f32 = jnp.float32
    nrm = lambda k, shape, scale: jax.random.normal(k, shape, f32) * scale
    L, D = DEPTH, D_MODEL
    return {
        'x': nrm(ks[0], (BATCH, SEQ, D), 1.0),
        'c': nrm(ks[1], (BATCH, D), 1.0),
        'norm_mix_gain': 1.0 + nrm(ks[2], (L, D), 0.05),
        'norm_ffn_gain': 1.0 + nrm(ks[3], (L, D), 0.05),
        'w_mod': nrm(ks[4], (L, D, 6 * D), 0.5 * D ** -0.5),
        'b_mod': nrm(ks[5], (L, 6 * D), 0.02),
        'w_in': nrm(ks[6], (L, D, IN_W), D ** -0.5),
        'w_out': nrm(ks[7], (L, MIX_W, D), MIX_W ** -0.5),
        'pool_w': nrm(ks[8], (L, len(POOL_WINDOWS), POOL_GROUP, POOL_GROUP), POOL_GROUP ** -0.5),
        'pool_scale': 1.0 + nrm(ks[9], (L, POOL_W), 0.1),
        'gla_w_gk_up': nrm(ks[10], (L, GLA_RANK, GLA_HEADS * GLA_DK), GLA_RANK ** -0.5),
        'gla_b_gk': nrm(ks[11], (L, GLA_HEADS * GLA_DK), 0.02),
        'gla_norm_gain': 1.0 + nrm(ks[12], (L, GLA_DV), 0.05),
        'nsa_q_gain': 1.0 + nrm(ks[13], (L, NSA_HEAD_DIM), 0.05),
        'nsa_k_gain': 1.0 + nrm(ks[14], (L, 3, NSA_HEAD_DIM), 0.05),
        'nsa_cmp_pos': nrm(ks[15], (L, 2, CMP_BLOCK, NSA_HEAD_DIM), 0.02),
        'nsa_cmp_w1': nrm(ks[16], (L, 2, CMP_BLOCK * NSA_HEAD_DIM, CMP_HIDDEN), (CMP_BLOCK * NSA_HEAD_DIM) ** -0.5),
        'nsa_cmp_w2': nrm(ks[17], (L, 2, CMP_HIDDEN, NSA_HEAD_DIM), CMP_HIDDEN ** -0.5),
        'w_ffn_in': nrm(ks[18], (L, D, 2 * FFN_HIDDEN), D ** -0.5),
        'w_ffn_out': nrm(ks[19], (L, FFN_HIDDEN, D), FFN_HIDDEN ** -0.5),
    }

def reference(x, c, norm_mix_gain, norm_ffn_gain, w_mod, b_mod, w_in, w_out, pool_w, pool_scale,
              gla_w_gk_up, gla_b_gk, gla_norm_gain, nsa_q_gain, nsa_k_gain, nsa_cmp_pos,
              nsa_cmp_w1, nsa_cmp_w2, w_ffn_in, w_ffn_out):
    b, s, _ = x.shape
    c_act = jax.nn.silu(c)
    split_at = [int(v) for v in np.cumsum(IN_SIZES)[:-1]]
    G = NSA_GROUPS
    heads = lambda a, n: a.reshape(b, s, n, NSA_HEAD_DIM)
    for l in range(DEPTH):
        mod = c_act @ w_mod[l] + b_mod[l]
        sh_a, sc_a, g_a, sh_f, sc_f, g_f = jnp.split(mod, 6, axis=-1)

        hmix = modulate(rms_norm(x, norm_mix_gain[l]), sh_a, sc_a)
        proj = hmix @ w_in[l]
        (u, gla_q, gla_k, gla_v, gla_g, gla_low, nsa_q, kc, vc, ksl, vsl, kwn, vwn,
         nsa_g) = jnp.split(proj, split_at, axis=-1)

        pool_out = pool_mixer(u, pool_w[l], pool_scale[l])

        log_a = jax.nn.log_sigmoid((gla_low @ gla_w_gk_up[l] + gla_b_gk[l]).astype(jnp.float32)) / GLA_GATE_NORM
        o_gla = gla_chunked(gla_q.reshape(b, s, GLA_HEADS, GLA_DK) * GLA_DK ** -0.5,
                            gla_k.reshape(b, s, GLA_HEADS, GLA_DK),
                            gla_v.reshape(b, s, GLA_HEADS, GLA_DV),
                            log_a.reshape(b, s, GLA_HEADS, GLA_DK))
        gla_out = rms_norm(o_gla, gla_norm_gain[l]).reshape(b, s, GLA_W) * jax.nn.silu(gla_g)

        kg = nsa_k_gain[l]
        q = rms_norm(heads(nsa_q, NSA_HEADS), nsa_q_gain[l]) * NSA_HEAD_DIM ** -0.5
        nsa_out = nsa_attention(q, heads(kc, G), heads(vc, G),
                                rms_norm(heads(ksl, G), kg[1]), heads(vsl, G),
                                rms_norm(heads(kwn, G), kg[2]), heads(vwn, G),
                                jax.nn.sigmoid(nsa_g).reshape(b, s, NSA_HEADS, 3),
                                nsa_cmp_pos[l], nsa_cmp_w1[l], nsa_cmp_w2[l], kg[0])

        mix = jnp.concatenate([pool_out, gla_out, nsa_out], axis=-1) @ w_out[l]
        x = x + g_a[:, None, :] * mix

        hf = modulate(rms_norm(x, norm_ffn_gain[l]), sh_f, sc_f)
        gate_h, up_h = jnp.split(hf @ w_ffn_in[l], 2, axis=-1)
        x = x + g_f[:, None, :] * ((jax.nn.silu(gate_h) * up_h) @ w_ffn_out[l])
    return x


_drawn_inputs = setup_inputs


def setup_inputs(seed=0):
    import zlib

    import numpy as np

    out = dict(_drawn_inputs(seed))
    spreads = {}
    factors = {'norm_mix_gain': 4.135,
     'norm_ffn_gain': 3.877,
     'pool_scale': 4.072,
     'gla_w_gk_up': 3.573,
     'gla_b_gk': 38.889,
     'gla_norm_gain': 8.0,
     'nsa_q_gain': 8.0,
     'nsa_k_gain': 8.0,
     'nsa_cmp_pos': 34.26}
    for name, (base, spread) in spreads.items():
        noise = np.random.default_rng([zlib.crc32(name.encode()), seed]).standard_normal(out[name].shape)
        drawn = base * np.exp(spread * noise) if base else spread * noise
        out[name] = jnp.asarray(drawn.astype(out[name].dtype))
    for name, factor in factors.items():
        out[name] = (out[name] * factor).astype(out[name].dtype)
    return out
```

```python
from contextlib import ExitStack

import numpy as np
import concourse.bass as bass
from concourse import mybir

P = 128
D = 2048
S = 512
T = S // P
KD = D // P
U = 512
FFN = -(-8 * D // (3 * 256)) * 256
FG = FFN // (4 * P)
H, G, DH = 16, 4, 64
R = H // G
NCMP = 32
CST = 16
LH = 4
LEVELS = (64, 32, 16, 8, 4, 2, 1)
POOL_WINDOWS = (2, 4, 8, 16)
EPS = 1e-6
FAR = 1e30

UNITS_IN = 16 + 4 + 8 * KD
UNITS_OUT = 4 * KD
UNITS_FFN = 2 * KD + 16
UNITS = -(-(UNITS_IN + UNITS_OUT + FG * UNITS_FFN) // 8) * 8
RAW = 8
SPLIT = 4

V_C, V_GMIX, V_GFFN, V_B, V_GKB, V_PSC, V_SLOPE, V_POS, V_END = 0, 16, 32, 48, 112, 114, 118, 134, 166
R_QG, R_KG, R_GLA, R_END = 0, 64, 256, 384

F32, F32R, U32 = mybir.dt.float32, mybir.dt.float32r, mybir.dt.uint32
ALU = mybir.AluOpType
ACT = mybir.ActivationFunctionType
AX = mybir.AxisListType


class Chain:

    def __init__(self, eng, sem):
        self.eng, self.sem, self.n, self.off = eng, sem, 0, 0

    def __call__(self, ins):
        self.n += 1
        ins.then_inc(self.sem, 1)
        self.eng.wait_ge(self.sem, self.off + self.n)

    def enter(self, i, per):
        self.start, self.per, self.off = self.n, per, i * per

    def leave(self, count):
        assert self.n - self.start == self.per, (self.n - self.start, self.per)
        self.n, self.off = self.start + count * self.per, 0


def layer_kernel(nc, x, wstream, mstream, vecs, rows, grow_bias, tabs, cmp_tab, up, pool_w, w1, w2, out):
    with ExitStack() as ctx:
        def sem(name):
            return ctx.enter_context(nc.semaphore(name))

        place = [16512]

        def at(name, shape, dt=F32, offset=None):
            size = int(np.prod(shape[1:])) * 4
            if offset is None:
                offset = place[0]
                place[0] += -(-size // 32) * 32
            assert offset + size <= 229344, name
            return nc.alloc_sbuf_tensor_at(name, shape, dt, offset=offset)

        raw = at("raw", [P, RAW, U])
        whi = at("whi", [P, SPLIT, U], F32R)
        wlo = at("wlo", [P, SPLIT, U], F32R)
        ident = at("ident", [P, P])
        ones = at("ones", [P, P])
        grow = at("grow", [P, 2 * D])
        vec = at("vec", [P, V_END])
        cact = at("cact", [P, KD])
        modc = at("modc", [P, 64])
        acol = at("acol", [P, KD])
        ss = at("ss", [P, 16])
        rstd = at("rstd", [P, 16])
        pbase = place[0]
        abase = pbase + 4 * (T * 4096 + 4 * S + S)
        mbase = abase + 2 * KD * S * 4
        xin = at("xin", [P, T, D], F32, pbase)
        xT = at("xT", [P, KD, S], F32, pbase + T * D * 4)
        modw = at("modw", [P, 4, 2 * U], F32, mbase)
        macc = at("macc", [P, U], F32, mbase + 4 * 2 * U * 4)
        hmH = at("hmH", [P, KD, S], F32R, abase)
        hmL = at("hmL", [P, KD, S], F32R, abase + KD * S * 4)
        htmp = at("htmp", [P, 2, S], F32, mbase)
        proj = at("proj", [P, T, 4096], F32, pbase)
        qkT = at("qkT", [P, 4, S], F32, pbase + 4 * T * 4096)
        lgT = at("lgT", [P, S], F32, pbase + 4 * (T * 4096 + 4 * S))
        poolT = at("poolT", [P, 4, S], F32, pbase + 4 * T * 4096)
        place[0] = mbase
        ptab = at("ptab", [P, 12, P])
        gmask = at("gmask", [P, 8, P])
        dist = at("dist", [P, S])
        row = at("row", [P, R_END])
        poolw = at("poolw", [P, 4 * P])
        upw = at("upw", [P, 2 * P])
        place[0] = abase
        bb = [at(f"bb{i}", [P, 2, S]) for i in range(2)]
        ee = [at(f"ee{i}", [P, 2, S]) for i in range(2)]
        qd = [at(f"qd{i}", [P, 2, S]) for i in range(2)]
        kd = [at(f"kd{i}", [P, 2, S]) for i in range(2)]
        att = at("att", [P, T * LH, P])
        kdN = at("kdN", [P, T, 2 * P])
        state = at("state", [P, 2, 2 * P])
        elast = at("elast", [P, 2, T])
        gN = at("gN", [P, T, 64], F32, mbase + 4 * (12 * P + 8 * P + S + R_END + 4 * P + 2 * P))
        poolD = at("poolD", [P, 4, S], F32, abase)
        gsq = at("gsq", [P, T, S], F32, abase)
        place[0] = abase
        cmpb = at("cmpb", [P, T, H * NCMP])
        bd = at("bd", [P, G, R * DH])
        kcT = at("kcT", [P, P])
        nbase = place[0]
        w1s = at("w1s", [P, KD, 2 * P])
        w2s = at("w2s", [P, 2, 2, DH])
        dup = at("dup", [P, T, G * 2 * DH])
        xs = at("xs", [P, G, 544])
        gt = at("gt", [P, 16, P])
        hid = at("hid", [P, 2, P])
        hrep = at("hrep", [P, 2, P])
        kcn = at("kcn", [P, 2, DH])
        place[0] = nbase
        qn = at("qn", [P, T, R * DH])
        kn = at("kn", [P, 2, T, 2 * DH])
        qT = at("qT", [P, 2, S])
        kT = at("kT", [P, 2, S])
        biasT = at("biasT", [P, R, S])
        sbuf = at("sbuf", [P, 3, S])
        pbuf = at("pbuf", [P, 2, S])
        pT = at("pT", [P, 2, S])
        sqs = at("sqs", [P, T, (R + 2) * DH])
        sc = at("sc", [P, R * NCMP])
        pc = at("pc", [P, R * NCMP])
        pcT = at("pcT", [P, P])
        kcg = at("kcg", [P, NCMP])
        mneg = at("mneg", [P, T * R * 2])
        den = at("den", [P, T, R, 3])
        coef = at("coef", [P, T, R, 3])
        mc = at("mc", [P, R])
        qss = at("qss", [P, T * (R + 2)])
        oacc = at("oacc", [P, 3, R * DH])
        mixH = at("mixH", [P, KD, S], F32R, abase)
        mixL = at("mixL", [P, KD, S], F32R, abase + KD * S * 4)
        hfH = at("hfH", [P, KD, S], F32R, abase)
        hfL = at("hfL", [P, KD, S], F32R, abase + KD * S * 4)
        x1 = at("x1", [P, T, D], F32, pbase)
        xn = at("xn", [P, T, D], F32, pbase + 4 * T * D)
        huH = at("huH", [P, 4, S], F32R, pbase + 4 * T * D)
        huL = at("huL", [P, 4, S], F32R, pbase + 4 * (T * D + 4 * S))
        dtmp = at("dtmp", [P, 2, S], F32, mbase)
        gsil = at("gsil", [P, 2, S], F32, mbase + 4 * 2 * S)
        hfull = at("hfull", [P, 2, S], F32, mbase + 4 * 4 * S)

        ps = ctx.enter_context(nc.psum_tensor("ps", [P, 8, U], F32))

        raw_landed = [sem(f"raw_landed{i}") for i in range(4)]
        mod_landed = [sem(f"mod_landed{i}") for i in range(4)]
        unit_hi, unit_ready, unit_used = sem("unit_hi"), sem("unit_ready"), sem("unit_used")
        dve_steps = sem("dve_steps")
        tile_done, proj_saved = sem("tile_done"), sem("proj_saved")
        x_landed, small_landed, g_landed = sem("x_landed"), sem("small_landed"), sem("g_landed")
        act_own, dve_own = sem("act_own"), sem("dve_own")
        sq_ready, var_ready, std_ready, rstd_ready = sem("sq_ready"), sem("var_ready"), sem("std_ready"), sem("rstd_ready")
        xn_ready, xt_psum, xt_saved = sem("xn_ready"), sem("xt_psum"), sem("xt_saved")
        cact_ready = sem("cact_ready")
        mod_used, mod_summed, hm_ready = sem("mod_used"), sem("mod_summed"), sem("hm_ready")
        mod_done = sem("mod_done")
        gla_const, nsa_const, w1_landed = sem("gla_const"), sem("nsa_const"), sem("w1_landed")
        pe_gla, dve_gla, act_gla = sem("pe_gla"), sem("dve_gla"), sem("act_gla")
        lev_e, lev_exp, lev_qk, lev_att, lev_cp = sem("lev_e"), sem("lev_exp"), sem("lev_qk"), sem("lev_att"), sem("lev_cp")
        st_psum, st_ready, kd_psum, kd_saved, o_psum = (sem("st_psum"), sem("st_ready"), sem("kd_psum"),
                                                       sem("kd_saved"), sem("o_psum"))
        pool_pe, pool_act = sem("pool_pe"), sem("pool_act")
        c_dup, c_psum, c_saved, c_gt, c_hid, c_hsaved, c_out, c_dve, c_act = (
            sem(n) for n in ("c_dup", "c_psum", "c_saved", "c_gt", "c_hid", "c_hsaved", "c_out", "c_dve", "c_act"))
        n_sq, n_ssq, n_std, n_qk, n_tr, n_trs, n_bias = (sem(n) for n in (
            "n_sq", "n_ssq", "n_std", "n_qk", "n_tr", "n_trs", "n_bias"))
        s_psum, s_saved, p_ready, pt_psum, pt_saved, pv_done = (sem(n) for n in (
            "s_psum", "s_saved", "p_ready", "pt_psum", "pt_saved", "pv_done"))
        cs_psum, cs_ready, cp_ready, cpt_psum, cpt_saved, cpv_done, o_saved = (sem(n) for n in (
            "cs_psum", "cs_ready", "cp_ready", "cpt_psum", "cpt_saved", "cpv_done", "o_saved"))
        m_psum, m_hi, m_lo, mixed = sem("m_psum"), sem("m_hi"), sem("m_lo"), sem("mixed")
        x1_landed, x1_ready, f_sq, f_var, f_std, f_rstd, f_xn, f_psum, f_ready = (sem(n) for n in (
            "x1_landed", "x1_ready", "f_sq", "f_var", "f_std", "f_rstd", "f_xn", "f_psum", "f_ready"))
        gate_done, gate_saved, up_saved, h_hi, h_lo, y_done, y_added = (sem(n) for n in (
            "gate_done", "gate_saved", "up_saved", "h_hi", "h_lo", "y_done", "y_added"))
        stored, cs_half = sem("stored"), sem("cs_half")

        block = ctx.enter_context(nc.Block())

        U_LG, U_N, U_OUT, U_FFN = 16, 20, UNITS_IN, UNITS_IN + UNITS_OUT

        TD_FFN = 3 * 9 + 3 * 4

        @block.sync
        def _(sp):
            def load_units(j, slot, wait=True):
                if wait:
                    sp.wait_ge(unit_ready, 2 * j - 6)
                sp.dma_start(raw[:, 2 * slot:2 * slot + 2, :].rearrange("p a b -> p (a b)"),
                             wstream[bass.ds(j * P, P), :]).then_inc(raw_landed[slot], 16)

            def load_mod(m, slot, wait=True):
                if wait:
                    sp.wait_ge(mod_used, m - 3)
                sp.dma_start(modw[:, slot, :], mstream[bass.ds(m * P, P), :]).then_inc(mod_landed[slot], 16)

            sp.dma_start(vec[:, :], vecs).then_inc(small_landed, 16)
            sp.dma_start(ident[:, :], tabs[:, 0:P]).then_inc(small_landed, 16)
            sp.dma_start(ones[:, :], tabs[:, P:2 * P]).then_inc(small_landed, 16)
            for t in range(T):
                sp.dma_start(xin[:, t, :], x[t * P:(t + 1) * P, :]).then_inc(x_landed, 16)
            for m in range(4):
                load_mod(m, m, wait=False)
            sp.dma_start(grow[:, :], grow_bias.partition_broadcast(P)).then_inc(g_landed, 16)
            for j in range(4):
                load_units(j, j, wait=False)
            with sp.Fori(1, 16) as i:
                for s in range(4):
                    load_mod(4 * i + s, s)
            with sp.Fori(0, 2) as i:
                for s in range(4):
                    load_units(4 * i + 4 + s, s)
            with sp.Fori(0, 16) as i:
                for s in range(4):
                    load_units(4 * i + 12 + s, s)
                    load_mod(8 * i + 64 + 2 * s, 2 * s % 4)
                    load_mod(8 * i + 65 + 2 * s, (2 * s + 1) % 4)
            with sp.Fori(0, (UNITS // 2 - 76) // 4) as i:
                for s in range(4):
                    load_units(4 * i + 76 + s, s)
            sp.wait_ge(y_added, 4 + 16 * FG)
            for t in range(T):
                sp.dma_start(out[t * P:(t + 1) * P, :], x1[:, t, :]).then_inc(stored, 16)
            sp.wait_ge(stored, 16 * T)

        @block.gpsimd
        def _(pool):
            with pool.Fori(0, UNITS // 8) as i:
                for r in range(8):
                    s = r % SPLIT
                    pool.wait_ge(unit_hi, 8 * i + r + 1)
                    nc.gpsimd.tensor_tensor(wlo[:, s, :], raw[:, r, :], whi[:, s, :].bitcast(F32),
                                            ALU.subtract).then_inc(unit_ready, 1)

        def used(u):
            return u + SPLIT

        @block.tensor
        def _(pe):
            def passes(acc, xa, xb, wa, wb, x_stationary, first, last):
                for n, (xo, wo) in enumerate(((xa, wa), (xb, wa), (xa, wb))):
                    lhs, rhs = (xo, wo) if x_stationary else (wo, xo)
                    ins = nc.tensor.matmul(acc, lhs, rhs, start=first and n == 0, stop=last and n == 2)
                return ins

            def token_block(u0, xH, xL, nk, bank, free, x_ready=None, after=None):
                for k in range(nk):
                    s = k % SPLIT
                    pe.wait_ge(unit_ready, u0 + (k + 1))
                    if x_ready is not None:
                        pe.wait_ge(*x_ready(k))
                    for t in range(T):
                        if k == 0:
                            pe.wait_ge(*free(t))
                        tok = slice(t * P, (t + 1) * P)
                        ins = passes(ps[:, bank + t, :], xH[:, k, tok], xL[:, k, tok], whi[:, s, :], wlo[:, s, :],
                                     True, k == 0, k == nk - 1)
                        if t == T - 1:
                            ins.then_inc(unit_used, 1)
                        elif k == nk - 1:
                            ins.then_inc(tile_done, 1)
                    if after is not None:
                        after(k)

            def column_block(u0, xH, xL, free, x_ready=None):
                for k in range(KD):
                    s = k % SPLIT
                    pe.wait_ge(unit_ready, u0 + (k + 1))
                    if x_ready is not None:
                        pe.wait_ge(*x_ready(k))
                    for c in range(4):
                        if k == 0 and free is not None:
                            pe.wait_ge(*free(c))
                        col = slice(c * P, (c + 1) * P)
                        ins = passes(ps[:, c, :], xH[:, k, :], xL[:, k, :], whi[:, s, col], wlo[:, s, col],
                                     False, k == 0, k == KD - 1)
                        if c == 3:
                            ins.then_inc(unit_used, 1)
                        elif k == KD - 1:
                            ins.then_inc(tile_done, 1)

            pe.wait_ge(small_landed, 48)
            pe.wait_ge(xn_ready, T)
            for k in range(KD):
                if k >= 4:
                    pe.wait_ge(xt_saved, k - 3)
                for t in range(T):
                    ins = nc.tensor.transpose(ps[:, k % 4, t * P:(t + 1) * P], xin[:, t, k * P:(k + 1) * P], ident[:, :])
                ins.then_inc(xt_psum, 1)

            def sum_columns(q):
                pe.wait_ge(mod_used, 8 * q + 8)
                for j in range(4):
                    ins = nc.tensor.matmul(ps[:, 7, j:j + 1], macc[:, j * P:(j + 1) * P], ones[:, 0:1],
                                           start=True, stop=True)
                ins.then_inc(mod_summed, 1)

            def sum_rows(q):
                pe.wait_ge(mod_used, 8 * q + 8)
                nc.tensor.matmul(ps[:, 7, :], ones[:, :], macc[:, :], start=True, stop=True).then_inc(mod_summed, 1)

            with pe.Fori(0, 8) as i:
                sum_columns(i)

            column_block(0, hmH, hmL, lambda c: (xt_saved, KD), lambda k: (hm_ready, k + 1))
            for k in range(KD):
                if k % 4 == 0:
                    pe.wait_ge(unit_ready, U_LG + k // 4 + 1)
                col = slice((k % 4) * 64, (k % 4) * 64 + 64)
                ins = passes(ps[0:64, 4, :], hmH[:, k, :], hmL[:, k, :], whi[:, k // 4, col], wlo[:, k // 4, col],
                             False, k == 0, k == KD - 1)
                if k % 4 == 3:
                    ins.then_inc(unit_used, 1)

            for half, summing in ((0, sum_rows), (1, sum_columns)):
                with pe.Fori(4 * half, 4 * half + 4) as i:
                    def between(k):
                        if k == 7:
                            summing(8 + 2 * i)
                        elif k == 15:
                            summing(9 + 2 * i)
                    token_block(U_N + KD * i, hmH, hmL, KD, 0, lambda t: (proj_saved, 4 * i + t + 1), after=between)

            pe.wait_ge(gla_const, 16 * 6)
            pe.wait_ge(proj_saved, 36)
            pe.wait_ge(act_gla, 1)
            for f in range(2):
                ins = nc.tensor.matmul(ps[:, f, :], upw[0:16, f * P:(f + 1) * P], lgT[0:16, :], start=True, stop=True)
            ins.then_inc(pe_gla, 1)
            for t in range(T):
                ins = nc.tensor.transpose(ps[:, 5, t * 64:(t + 1) * 64], lgT[0:64, t * P:(t + 1) * P], ident[0:64, 0:64])
            ins.then_inc(pe_gla, 1)

            def level(l, q_, k_):
                for n in range(4):
                    p0 = (n % 2) * 64
                    for c in range(4):
                        tok = slice((2 * (n // 2) + c // 2) * P, (2 * (n // 2) + c // 2 + 1) * P)
                        ins = nc.tensor.matmul(ps[:, 4 * (l % 2) + n, c * P:(c + 1) * P], k_[p0:p0 + 64, c % 2, tok],
                                               q_[p0:p0 + 64, c % 2, tok], start=True, stop=True)
                    ins.then_inc(lev_att, 1)

            pe.wait_ge(dve_gla, 1)
            pe.wait_ge(act_gla, 2)
            level(0, qkT[:, 0:2, :], qkT[:, 2:4, :])
            for l in range(1, 8):
                pe.wait_ge(lev_qk, l)
                if l >= 2:
                    pe.wait_ge(lev_cp, 4 * (l - 1))
                level(l, qd[l % 2], kd[l % 2])
            pe.wait_ge(lev_qk, 8)
            pe.wait_ge(lev_cp, 28)
            for t in range(T):
                for f in range(2):
                    ins = nc.tensor.transpose(ps[:, t // 2, (t % 2) * 256 + f * P:(t % 2) * 256 + (f + 1) * P],
                                              kd[0][:, f, t * P:(t + 1) * P], ident[:, :])
            ins.then_inc(kd_psum, 1)
            pe.wait_ge(kd_saved, 2)
            pe.wait_ge(lev_cp, 32)
            for t in range(T):
                if t:
                    pe.wait_ge(st_ready, t)
                for f in range(2):
                    if t:
                        nc.tensor.matmul(ps[:, t, f * 256:(f + 1) * 256], qd[0][:, f, t * P:(t + 1) * P], state[:, f, :],
                                         start=True, stop=False)
                    for h in (2 * f, 2 * f + 1):
                        a_h = att[:, 8 * (t // 2) + 4 * (h % 2) + 2 * (t % 2) + f, :]
                        ins = nc.tensor.matmul(ps[:, t, h * P:(h + 1) * P], a_h,
                                               proj[:, t, 512 + h * P:512 + (h + 1) * P],
                                               start=t == 0, stop=t == 0 or h % 2 == 1)
                ins.then_inc(o_psum, 1)
                if t < T - 1:
                    for h in range(LH):
                        f, p0 = h // 2, (h % 2) * 64
                        v_h = proj[:, t, 512 + h * P:512 + (h + 1) * P]
                        ins = nc.tensor.matmul(ps[p0:p0 + 64, 4 + t, h * P:(h + 1) * P], kdN[:, t, h * 64:(h + 1) * 64],
                                               v_h, start=True, stop=True)
                    ins.then_inc(st_psum, 1)

            for g in range(4):
                pe.wait_ge(dve_gla, 3)
                u_g = slice(g * P, (g + 1) * P)
                for t in range(T):
                    first = ptab[:, 3 * g + (0 if t == 0 else 1), :]
                    ins = nc.tensor.matmul(ps[:, g, t * P:(t + 1) * P], proj[:, t, u_g], first, start=True, stop=t == 0)
                    if t:
                        ins = nc.tensor.matmul(ps[:, g, t * P:(t + 1) * P], proj[:, t - 1, u_g], ptab[:, 3 * g + 2, :],
                                               start=False, stop=True)
                ins.then_inc(pool_pe, 1)
            for g in range(4):
                pe.wait_ge(pool_act, g + 1)
                nc.tensor.matmul(ps[:, 4 + g, :], poolw[:, g * P:(g + 1) * P], poolD[:, g, :],
                                 start=True, stop=True).then_inc(pool_pe, 1)

            for v in range(2):
                pe.wait_ge(c_dup, v + 1)
                for g in range(G):
                    if v:
                        pe.wait_ge(c_saved, g + 1)
                    else:
                        pe.wait_ge(pool_act, 4)
                    for t in range(T):
                        ins = nc.tensor.transpose(ps[:, g, t * P:(t + 1) * P], dup[:, t, g * P:(g + 1) * P], ident[:, :])
                    ins.then_inc(c_psum, 1)
                pe.wait_ge(w1_landed, 16 * (v + 1))
                pe.wait_ge(nsa_const, 16 * 2)
                pe.wait_ge(pool_act, 8)
                if v:
                    pe.wait_ge(c_dve, 2)
                for i in range(16):
                    pe.wait_ge(c_gt, 16 * v + i + 1)
                    for m in range(2):
                        ins = nc.tensor.matmul(ps[:, 4 + m, 0:P], w1s[:, i, m * P:(m + 1) * P], gt[:, i, :],
                                               start=i == 0, stop=i == 15)
                ins.then_inc(c_hid, 1)
                pe.wait_ge(c_hsaved, v + 1)
                if v == 0:
                    for m in range(2):
                        ins = nc.tensor.matmul(ps[:, 6, 0:DH], hid[:, m, :], w2s[:, 0, m, :], start=m == 0, stop=m == 1)
                    ins.then_inc(c_out, 1)
                    pe.wait_ge(c_dve, 1)
                    nc.tensor.transpose(ps[:, 7, 0:P], kcn[:, :, :].rearrange("p a b -> p (a b)"),
                                        ident[:, :]).then_inc(c_out, 1)
                else:
                    for g in range(G):
                        pe.wait_ge(c_act, g + 1)
                        for m in range(2):
                            ins = nc.tensor.matmul(ps[:, 6 + g % 2, 0:DH], hrep[:, m, :], w2s[:, 1, m, :],
                                                   start=m == 0, stop=m == 1)
                        ins.then_inc(c_out, 1)

            units = [(t, r, b) for t in range(T) for r in range(R) for b in range(2)]
            NU = len(units)
            with pe.Fori(0, G) as g:
                pe.wait_ge(n_qk, g + 1)
                pe.wait_ge(o_saved, 4 * g + 4)
                for a in range(2):
                    for t in range(T):
                        ins = nc.tensor.transpose(ps[:, a, t * P:(t + 1) * P], qn[:, t, a * P:(a + 1) * P], ident[:, :])
                    ins.then_inc(n_tr, 1)
                for b in range(2):
                    for t in range(T):
                        ins = nc.tensor.transpose(ps[:, 3 + b, t * P:(t + 1) * P], kn[:, b, t, :], ident[:, :])
                    ins.then_inc(n_tr, 1)
                pe.wait_ge(n_trs, 4 * g + 4)

                def scores(n):
                    t, r, b = units[n]
                    if n >= 3:
                        pe.wait_ge(s_saved, 32 * g + (n - 2))
                    p0 = (r % 2) * 64
                    w = (t + 1) * P
                    nc.tensor.matmul(ps[:, n % 3, 0:w], qT[p0:p0 + 64, r // 2, t * P:(t + 1) * P],
                                     kT[p0:p0 + 64, b, 0:w], start=True, stop=True).then_inc(s_psum, 1)

                def cmp_scores(t):
                    if t:
                        pe.wait_ge(o_saved, 4 * g + t + 4)
                    for r in (0, 2, 1, 3):
                        if r == 1:
                            ins.then_inc(cs_half, 1)
                            pe.wait_ge(cs_half, 4 * g + (t + 1))
                        p0 = (r % 2) * 64
                        ins = nc.tensor.matmul(ps[:, 7, r * NCMP:(r + 1) * NCMP],
                                               qT[p0:p0 + 64, r // 2, t * P:(t + 1) * P],
                                               kcg[p0:p0 + 64, :], start=True, stop=True)
                    ins.then_inc(cs_psum, 1)

                def transposes(n):
                    t, r, b = units[n]
                    pe.wait_ge(p_ready, 32 * g + (n + 1))
                    if n >= 2:
                        pe.wait_ge(pt_saved, 32 * g + (n - 1))
                    for c in range(t + 1):
                        ins = nc.tensor.transpose(ps[:, 3 + n % 2, c * P:(c + 1) * P], pbuf[:, n % 2, c * P:(c + 1) * P],
                                                  ident[:, :])
                    ins.then_inc(pt_psum, 1)

                def values(n):
                    t, r, b = units[n]
                    pe.wait_ge(pt_saved, 32 * g + (n + 1))
                    if r == 0 and b == 0 and t >= 2:
                        pe.wait_ge(o_saved, 4 * g + t + 3)
                    for c in range(t + 1):
                        v_b = proj[:, c, bass.ds(3072 + 512 * b + 256 + g * DH, DH)]
                        ins = nc.tensor.matmul(ps[:, 5 + t % 2, b * 256 + r * DH:b * 256 + (r + 1) * DH],
                                               pT[:, n % 2, c * P:(c + 1) * P], v_b, start=c == 0, stop=c == t)
                    ins.then_inc(pv_done, 1)

                def cmp_values(t):
                    pe.wait_ge(cpt_saved, 4 * g + (t + 1))
                    nc.tensor.matmul(ps[:, 7, 256:512], pcT[:, :], bd[:, bass.ds(g, 1), :].rearrange("p a b -> p (a b)"),
                                     start=True, stop=True).then_inc(cpv_done, 1)

                scores(0)
                scores(1)
                for n in range(NU):
                    t, r, b = units[n]
                    if n + 2 < NU:
                        scores(n + 2)
                    if n % 8 == 4:
                        cmp_scores(t)
                    if n % 8 == 7:
                        pe.wait_ge(cp_ready, 4 * g + (t + 1))
                        nc.tensor.transpose(ps[:, 7, P:2 * P], pc[:, :], ident[:, :]).then_inc(cpt_psum, 1)
                    transposes(n)
                    if n >= 1:
                        values(n - 1)
                    if n % 8 == 0 and t:
                        cmp_values(t - 1)
                values(NU - 1)
                cmp_values(T - 1)

            pe.wait_ge(o_saved, 20)
            for k in range(4, KD):
                if k >= 12:
                    pe.wait_ge(m_lo, k - 7)
                c0 = 512 + (k - 4) * P if k < 8 else 1536 + (k - 8) * P
                for t in range(T):
                    ins = nc.tensor.transpose(ps[:, k % 8, t * P:(t + 1) * P], proj[:, t, c0:c0 + P], ident[:, :])
                ins.then_inc(m_psum, 1)
            pe.wait_ge(m_lo, KD)
            with pe.Fori(0, 4) as i:
                token_block(U_OUT + KD * i, mixH, mixL, KD, 0, lambda t: (x1_ready, 4 * i + t + 1))

            pe.wait_ge(f_xn, T)
            for k in range(KD):
                if k >= 8:
                    pe.wait_ge(f_ready, k - 7)
                for t in range(T):
                    ins = nc.tensor.transpose(ps[:, k % 8, t * P:(t + 1) * P], xn[:, t, k * P:(k + 1) * P], ident[:, :])
                ins.then_inc(f_psum, 1)
            pe.wait_ge(f_ready, KD)
            with pe.Fori(0, FG) as i:
                for a in range(2):
                    column_block(U_FFN + UNITS_FFN * i + KD * a, hfH, hfL,
                                 lambda c: (gate_saved, 4 * i + 2 * a + c + 1) if c < 2
                                 else (up_saved, 4 * i + 2 * a + c - 1))
                for c in range(4):
                    token_block(U_FFN + UNITS_FFN * i + 2 * KD + 4 * c, huH, huL, 4, 4,
                                lambda t: (y_added, 16 * i + 4 * c + t + 1),
                                (lambda k: (h_lo, 4 * i + (k + 1))) if c == 0 else None)

        @block.scalar
        def _(act):
            A = nc.scalar.activation

            def split(rounds, first, stop):
                for k in range(first, stop):
                    if k % 2 == 0:
                        act.wait_ge(raw_landed[k % 8 // 2], 16 * rounds + 16 * (k // 8 + 1))
                    act.wait_ge(unit_used, 8 * rounds + (k + 1))
                    A(whi[:, k % SPLIT, :], raw[:, k % 8, :], ACT.Copy).then_inc(unit_hi, 1)
            act.wait_ge(small_landed, 48)
            A(cact[:, :], vec[:, V_C:V_C + KD], ACT.Silu).then_inc(cact_ready, 1)
            act.wait_ge(x_landed, 16 * T)
            for t in range(T):
                ins = A(xT[:, 4 * t:4 * t + 4, :].rearrange("p a b -> p (a b)"), xin[:, t, :], ACT.Square,
                        accum_out=ss[:, t:t + 1])
            ins.then_inc(sq_ready, 1)
            act.wait_ge(var_ready, 1)
            A(rstd[:, 4:8], ss[:, 4:8], ACT.Sqrt).then_inc(std_ready, 1)
            act.wait_ge(rstd_ready, 1)
            act.wait_ge(sq_ready, 1)
            for t in range(T):
                A(xin[:, t, :], xin[:, t, :], ACT.Copy, scale=rstd[:, t:t + 1]).then_inc(xn_ready, 1)
            act.wait_ge(xn_ready, T)
            for k in range(KD):
                act.wait_ge(xt_psum, k + 1)
                A(xT[:, k, :], ps[:, k % 4, :], ACT.Copy).then_inc(xt_saved, 1)

            split(0, 0, 4)
            act.wait_ge(hm_ready, KD)
            split(0, 4, 19)
            for c in range(4):
                if c < 3:
                    act.wait_ge(tile_done, c + 1)
                else:
                    act.wait_ge(unit_used, used(16))
                A(qkT[:, c, :], ps[:, c, :], ACT.Copy, scale=DH ** -0.5 if c < 2 else 1.0).then_inc(proj_saved, 1)
                if c == 2:
                    split(0, 19, 20)
            split(0, 20, 24)
            act.wait_ge(unit_used, used(20))
            A(lgT[0:64, :], ps[0:64, 4, :], ACT.Copy).then_inc(act_gla, 1)
            with act.Fori(0, 8) as i:
                split(2 * i + 3, 0, 15)
                for t in range(T):
                    if t < 3:
                        act.wait_ge(tile_done, 3 * i + 3 + t + 1)
                    else:
                        act.wait_ge(unit_used, 16 * i + used(U_N + KD))
                    A(proj[:, t, bass.ds(512 * i, 512)], ps[:, t, :], ACT.Copy).then_inc(proj_saved, 1)
                    if t == 2:
                        split(2 * i + 3, 15, 16)

            act.wait_ge(mod_done, 1)
            o = 2 * P
            for dst, src in ((ptab[:, :, :].rearrange("p a b -> p (a b)"), tabs[:, o:o + 12 * P]),
                             (gmask[:, :, :].rearrange("p a b -> p (a b)"), tabs[:, o + 12 * P:o + 20 * P]),
                             (dist[:, :], tabs[:, o + 20 * P:o + 24 * P]),
                             (row[:, :], rows.partition_broadcast(P)),
                             (poolw[:, :], pool_w), (upw[0:16, :], up)):
                act.dma_start(dst, src).then_inc(gla_const, 16)

            act.wait_ge(pe_gla, 2)
            A(gN[:, :, :].rearrange("p a b -> p (a b)"), ps[:, 5, 0:256], ACT.Sigmoid).then_inc(act_gla, 1)
            act.wait_ge(dve_gla, 2)
            A(ee[1][:, :, :], ee[0][:, :, :], ACT.Exp).then_inc(act_gla, 1)
            act.wait_ge(act_gla, 3)
            A(ee[1][:, :, :], ee[1][:, :, :], ACT.Ln, bias=1.0).then_inc(act_gla, 1)
            for l in range(1, 8):
                act.wait_ge(lev_e, l)
                A(ee[l % 2][:, :, :], ee[l % 2][:, :, :], ACT.Exp).then_inc(lev_exp, 1)
            act.wait_ge(lev_e, 8)
            A(ee[0][:, :, :], ee[0][:, :, :], ACT.Exp)
            A(elast[:, :, :], elast[:, :, :], ACT.Exp)
            A(ee[1][:, :, :], bb[1][:, :, :], ACT.Exp).then_inc(lev_exp, 1)
            act.wait_ge(kd_psum, 1)
            for n in range(2):
                A(kdN[:, 2 * n:2 * n + 2, :].rearrange("p a b -> p (a b)"), ps[:, n, :], ACT.Copy).then_inc(kd_saved, 1)
            for t in range(T):
                A(proj[:, t, 1024:1536], proj[:, t, 1024:1536], ACT.Silu)
            act.wait_ge(st_ready, 3)
            act.wait_ge(o_psum, T)
            for t in range(T):
                ins = A(gsq[:, t, :], ps[:, t, :], ACT.Square)
            ins.then_inc(act_gla, 1)
            act.wait_ge(var_ready, 2)
            A(rstd[:, :], ss[:, :], ACT.Sqrt).then_inc(std_ready, 1)

            for g in range(4):
                act.wait_ge(pool_pe, g + 1)
                A(poolD[:, g, :], ps[:, g, :], ACT.Copy).then_inc(pool_act, 1)
            for g in range(4):
                act.wait_ge(pool_pe, 5 + g)
                A(poolT[:, g, :], ps[:, 4 + g, :], ACT.Copy, scale=vec[:, V_PSC + g:V_PSC + g + 1]).then_inc(pool_act, 1)

            act.wait_ge(pool_act, 8)
            act.dma_start(w1s[:, :, :].rearrange("p a b -> p (a b)"), w1[0]).then_inc(w1_landed, 16)
            act.dma_start(w2s[:, :, :, :].rearrange("p a b c -> p (a b c)"), w2).then_inc(nsa_const, 16)
            act.dma_start(cmpb[:, :, :].rearrange("p a b -> p (a b)"), cmp_tab).then_inc(nsa_const, 16)
            for v in range(2):
                if v:
                    act.wait_ge(c_psum, 4)
                for t in range(T):
                    src = proj[:, t, 2560 + v * 256:2560 + (v + 1) * 256].rearrange("p (g d) -> p g d", g=G)
                    dst = dup[:, t, :].rearrange("p (g a d) -> p g a d", g=G, a=2)
                    for a in range(2):
                        ins = A(dst[:, :, a, :], src, ACT.Copy)
                ins.then_inc(c_dup, 1)
                if v:
                    act.wait_ge(c_gt, 16)
                for g in range(G):
                    act.wait_ge(c_psum, 4 * v + g + 1)
                    A(xs[0:64, g, 0:S], ps[0:64, g, :], ACT.Copy)
                    A(xs[64:128, g, 0:S - 1], ps[64:128, g, 1:S], ACT.Copy).then_inc(c_saved, 1)
                act.wait_ge(c_hid, v + 1)
                if v == 0:
                    act.dma_start(w1s[:, :, :].rearrange("p a b -> p (a b)"), w1[1]).then_inc(w1_landed, 16)
                for m in range(2):
                    ins = A(hid[:, m, :], ps[:, 4 + m, 0:P], ACT.Silu)
                ins.then_inc(c_hsaved, 1)
                if v == 0:
                    act.wait_ge(var_ready, 3)
                    A(rstd[:, 0:1], ss[:, 0:1], ACT.Sqrt).then_inc(std_ready, 1)
                    act.wait_ge(c_out, 2)
                    A(kcT[:, :], ps[:, 7, 0:P], ACT.Copy).then_inc(c_dve, 1)
                else:
                    act.wait_ge(c_hsaved, 2)
                    for g in range(G):
                        if g:
                            act.wait_ge(c_out, 2 + g)
                        for r in range(R):
                            ins = A(hrep[:, :, r * 32:(r + 1) * 32], hid[:, :, g * 32:(g + 1) * 32], ACT.Copy)
                        ins.then_inc(c_act, 1)
                        act.wait_ge(c_out, 3 + g)
                        for r in range(R):
                            ins = A(bd[r * 32:(r + 1) * 32, g, r * DH:(r + 1) * DH],
                                    ps[r * 32:(r + 1) * 32, 6 + g % 2, 0:DH], ACT.Copy)
                    ins.then_inc(c_saved, 1)

            act.wait_ge(c_saved, 9)
            units = [(t, r, b) for t in range(T) for r in range(R) for b in range(2)]
            with act.Fori(0, G) as g:
                for t in range(T):
                    A(sqs[:, t, 0:256], proj[:, t, bass.ds(1536 + g * 256, 256)], ACT.Square)
                    A(sqs[:, t, 256:320], proj[:, t, bass.ds(3072 + g * DH, DH)], ACT.Square)
                    ins = A(sqs[:, t, 320:384], proj[:, t, bass.ds(3584 + g * DH, DH)], ACT.Square)
                ins.then_inc(n_sq, 1)
                act.wait_ge(n_ssq, g + 1)
                A(qss[:, :], qss[:, :], ACT.Sqrt).then_inc(n_std, 1)
                A(kcg[:, :], kcT[:, bass.ds(g * NCMP, NCMP)], ACT.Copy)
                for r in range(R):
                    ins = A(biasT[:, r, :], dist[:, :], ACT.Copy, scale=vec[:, bass.ds(V_SLOPE + g * R + r, 1)])
                ins.then_inc(n_bias, 1)
                for n in range(4):
                    act.wait_ge(n_tr, 4 * g + n + 1)
                    dst = qT[:, n, :] if n < 2 else kT[:, n - 2, :]
                    A(dst, ps[:, n if n < 2 else 1 + n, :], ACT.Copy).then_inc(n_trs, 1)

                def exps(n):
                    t, r, b = units[n]
                    w = (t + 1) * P
                    act.wait_ge(s_saved, 32 * g + (n + 1))
                    if n >= 2:
                        act.wait_ge(pt_psum, 32 * g + (n - 1))
                    A(pbuf[:, n % 2, 0:w], sbuf[:, n % 3, 0:w], ACT.Exp, bias=mneg[:, n:n + 1], scale=-1.0,
                      accum_out=den[:, t, r, 1 + b:2 + b]).then_inc(p_ready, 1)

                def save_pt(n):
                    t, r, b = units[n]
                    w = (t + 1) * P
                    act.wait_ge(pt_psum, 32 * g + (n + 1))
                    if n >= 2:
                        act.wait_ge(pv_done, 32 * g + (n - 1))
                    A(pT[:, n % 2, 0:w], ps[:, 3 + n % 2, 0:w], ACT.Copy).then_inc(pt_saved, 1)

                exps(0)
                for n in range(len(units)):
                    t = units[n][0]
                    if n + 1 < len(units):
                        exps(n + 1)
                    if n % 8 == 6:
                        act.wait_ge(cs_ready, 4 * g + (t + 1))
                        A(pc[:, :], sc[:, :], ACT.Exp, scale=-1.0).then_inc(cp_ready, 1)
                    if n % 8 == 7:
                        act.wait_ge(cpt_psum, 4 * g + (t + 1))
                        A(pcT[:, :], ps[:, 7, P:2 * P], ACT.Copy).then_inc(cpt_saved, 1)
                    save_pt(n)

            act.wait_ge(o_saved, 20)
            for k in range(KD):
                if k < 4:
                    src = poolT[:, k, :]
                else:
                    act.wait_ge(m_psum, k - 3)
                    src = ps[:, k % 8, :]
                A(mixH[:, k, :], src, ACT.Copy).then_inc(m_hi, 1)
            act.wait_ge(m_lo, KD)
            for t in range(T):
                act.dma_start(x1[:, t, :], x[t * P:(t + 1) * P, :]).then_inc(x1_landed, 16)
            with act.Fori(0, 4) as i:
                split(2 * i + (U_OUT + 4) // 8, 0, 16)
            act.wait_ge(x1_ready, 20)
            for t in range(T):
                ins = A(xn[:, t, :], x1[:, t, :], ACT.Square, accum_out=ss[:, t:t + 1])
            ins.then_inc(f_sq, 1)
            act.wait_ge(f_var, 1)
            A(rstd[:, 4:8], ss[:, 4:8], ACT.Sqrt).then_inc(f_std, 1)
            act.wait_ge(f_rstd, 1)
            for t in range(T):
                A(xn[:, t, :], x1[:, t, :], ACT.Copy, scale=rstd[:, t:t + 1]).then_inc(f_xn, 1)
            act.wait_ge(f_ready, KD)
            with act.Fori(0, FG) as i:
                rounds = 6 * i + (U_FFN + 4) // 8
                for a in range(2):
                    split(rounds, 16 * a, 16 * a + 15)
                    for c in range(2):
                        act.wait_ge(tile_done, TD_FFN + 18 * i + 3 * a + c + 1)
                        act.wait_ge(up_saved, 4 * i + 2 * a + c + 1)
                        A(gsil[:, c, :], ps[:, c, :], ACT.Silu).then_inc(gate_saved, 1)
                    split(rounds, 16 * a + 15, 16 * a + 16)
                    for c in range(2):
                        act.wait_ge(up_saved, 4 * i + 2 * a + c + 3)
                        act.wait_ge(tile_done, TD_FFN + 18 * i)
                        act.wait_ge(unit_used, UNITS_FFN * i + used(U_FFN))
                        A(huH[:, 2 * a + c, :], hfull[:, c, :], ACT.Copy).then_inc(h_hi, 1)
                split(rounds, 32, 48)

        @block.vector
        def _(dve):
            own = Chain(dve, dve_own)
            V = nc.vector
            V.memset(rstd[:, :], 0.0).then_inc(unit_used, SPLIT)
            dve.wait_ge(sq_ready, 1)
            V.tensor_scalar(ss[:, 4:8], ss[:, 0:4], 1.0 / D, EPS, ALU.mult, ALU.add).then_inc(var_ready, 1)
            dve.wait_ge(std_ready, 1)
            V.reciprocal(rstd[:, 0:4], rstd[:, 4:8]).then_inc(rstd_ready, 1)

            def add_mod(q):
                for d in range(8):
                    dve.wait_ge(mod_landed[d % 4], 32 * q + 16 * (d // 4 + 1))
                    for e in range(2):
                        k = 2 * d + e
                        src, scal = modw[:, d % 4, e * U:(e + 1) * U], cact[:, k:k + 1]
                        if k == 0:
                            own(V.tensor_scalar(macc[:, :], src, scal, None, ALU.mult))
                            continue
                        ins = V.scalar_tensor_tensor(out=macc[:, :], in0=src, scalar=scal, in1=macc[:, :],
                                                     op0=ALU.mult, op1=ALU.add)
                        if e == 0:
                            own(ins)
                        else:
                            ins.then_inc(mod_used, 1)
                            dve.wait_ge(mod_used, 8 * q + (d + 1))

            dve.wait_ge(cact_ready, 1)
            with dve.Fori(0, 8) as i:
                own.enter(i, 9)
                add_mod(i)
                dve.wait_ge(mod_summed, i + 1)
                own(V.tensor_tensor(modc[:, bass.ds(4 * i, 4)], ps[:, 7, 0:4], vec[:, bass.ds(V_B + 4 * i, 4)], ALU.add))
            own.leave(8)
            own(V.scalar_tensor_tensor(out=acol[:, :], in0=modc[:, 16:32], scalar=1.0, in1=vec[:, V_GMIX:V_GMIX + 16],
                                       op0=ALU.add, op1=ALU.mult))
            dve.wait_ge(xt_saved, KD)
            with dve.Fori(0, KD) as k:
                own.enter(k, 2)
                xk = xT[:, bass.ds(k, 1), :].rearrange("p a b -> p (a b)")
                hk = hmH[:, bass.ds(k, 1), :].rearrange("p a b -> p (a b)")
                lk = hmL[:, bass.ds(k, 1), :].rearrange("p a b -> p (a b)")
                own(V.tensor_scalar(xk, xk, acol[:, bass.ds(k, 1)], modc[:, bass.ds(k, 1)], ALU.mult, ALU.add))
                own(V.tensor_copy(hk, xk))
                V.tensor_tensor(lk, xk, hk.bitcast(F32), ALU.subtract).then_inc(hm_ready, 1)
            own.leave(KD)

            dve.wait_ge(g_landed, 16)
            with dve.Fori(0, 8) as i:
                own.enter(i, 9)
                add_mod(8 + i)
                dve.wait_ge(mod_summed, 9 + i)
                g_i = grow[:, bass.ds(512 * i, 512)]
                own(V.tensor_tensor(g_i, ps[:, 7, :], g_i, ALU.add))
            own.leave(8)
            with dve.Fori(0, 8) as i:
                own.enter(i, 9)
                add_mod(16 + i)
                dve.wait_ge(mod_summed, 17 + i)
                own(V.tensor_tensor(modc[:, bass.ds(32 + 4 * i, 4)], ps[:, 7, 0:4], vec[:, bass.ds(V_B + 32 + 4 * i, 4)],
                                    ALU.add))
            own.leave(8)
            V.scalar_tensor_tensor(out=acol[:, :], in0=modc[:, 48:64], scalar=1.0, in1=vec[:, V_GFFN:V_GFFN + 16],
                                   op0=ALU.add, op1=ALU.mult).then_inc(mod_done, 1)

            dve.wait_ge(proj_saved, 36)
            V.memset(att[:, :, :], 0.0)
            V.memset(state[:, :, :], 0.0)
            V.memset(qd[0][:, :, :], 0.0)
            V.memset(qd[1][:, :, :], 0.0)
            V.memset(kd[0][:, :, :], 0.0)
            own(V.memset(kd[1][:, :, :], 0.0))
            dve.wait_ge(pe_gla, 1)
            z, nz = bb[0], ee[0]
            for f in range(2):
                ins = V.tensor_scalar(z[:, f, :], ps[:, f, :], vec[:, V_GKB + f:V_GKB + f + 1], None, ALU.add)
            ins.then_inc(dve_gla, 1)
            dve.wait_ge(dve_gla, 1)
            V.scalar_tensor_tensor(out=nz[:, :, :], in0=z[:, :, :], scalar=-1.0, in1=z[:, :, :],
                                   op0=ALU.mult, op1=ALU.min).then_inc(dve_gla, 1)
            dve.wait_ge(act_gla, 4)
            own(V.scalar_tensor_tensor(out=bb[1][:, :, :], in0=z[:, :, :], scalar=0.0, in1=ee[1][:, :, :],
                                       op0=ALU.min, op1=ALU.subtract))
            own(V.tensor_scalar(bb[0][:, :, :], bb[1][:, :, :], 1.0 / 16.0, None, ALU.mult))
            cur = 0
            for step in (1, 2, 4, 8, 16, 32, 64):
                a = bb[cur][:, :, :].rearrange("p f (t s) -> p (f t) s", t=T)
                b = bb[1 - cur][:, :, :].rearrange("p f (t s) -> p (f t) s", t=T)
                V.tensor_tensor(b[:, :, step:P], a[:, :, step:P], a[:, :, 0:P - step], ALU.add)
                own(V.tensor_copy(b[:, :, 0:step], a[:, :, 0:step]))
                cur = 1 - cur
            assert cur == 1
            bc = bb[1][:, :, :].rearrange("p f s -> p (f s)")

            def copies(l):
                for t in range(T):
                    dve.wait_ge(lev_att, 4 * l + t + 1)
                    mask = gmask[:, l:l + 1, :].bitcast(U32).to_broadcast([P, LH, P])
                    src = ps[:, 4 * (l % 2) + t, :].rearrange("p (h i) -> p h i", h=LH)
                    if l:
                        dve.wait_ge(lev_cp, 4 * l - 4 + t + 1)
                    V.copy_predicated(att[:, t * LH:(t + 1) * LH, :], mask, src).then_inc(lev_cp, 1)

            for l, hs in enumerate(LEVELS, 1):
                e = ee[l % 2][:, :, :].rearrange("p f s -> p (f s)").rearrange("p (n a s) -> p n a s", a=2, s=hs)
                b = bc.rearrange("p (n a s) -> p n a s", a=2, s=hs)
                nb = 2 * S // (2 * hs)
                ref = b[:, :, 0, hs - 1:hs].to_broadcast([P, nb, hs])
                if l >= 2:
                    dve.wait_ge(lev_qk, l - 1)
                V.tensor_tensor(e[:, :, 0, :], ref, b[:, :, 0, :], ALU.subtract)
                V.tensor_tensor(e[:, :, 1, :], b[:, :, 1, :], ref, ALU.subtract).then_inc(lev_e, 1)
                copies(l - 1)
                dve.wait_ge(lev_exp, l)
                if l >= 3:
                    dve.wait_ge(lev_att, 4 * (l - 2) + 4)
                qv = qkT[:, 0:2, :].rearrange("p f s -> p (f s)").rearrange("p (n a s) -> p n a s", a=2, s=hs)
                kv = qkT[:, 2:4, :].rearrange("p f s -> p (f s)").rearrange("p (n a s) -> p n a s", a=2, s=hs)
                qo = qd[l % 2][:, :, :].rearrange("p f s -> p (f s)").rearrange("p (n a s) -> p n a s", a=2, s=hs)
                ko = kd[l % 2][:, :, :].rearrange("p f s -> p (f s)").rearrange("p (n a s) -> p n a s", a=2, s=hs)
                V.tensor_tensor(ko[:, :, 0, :], kv[:, :, 0, :], e[:, :, 0, :], ALU.mult)
                V.tensor_tensor(qo[:, :, 1, :], qv[:, :, 1, :], e[:, :, 1, :], ALU.mult).then_inc(lev_qk, 1)
            b = bb[1][:, :, :].rearrange("p f (t s) -> p (f t) s", t=T)
            e = ee[0][:, :, :].rearrange("p f (t s) -> p (f t) s", t=T)
            dve.wait_ge(lev_qk, 7)
            V.tensor_copy(elast[:, :, :].rearrange("p f t -> p (f t)"), b[:, :, P - 1])
            V.tensor_tensor(e, b[:, :, P - 1:P].to_broadcast([P, 2 * T, P]), b, ALU.subtract).then_inc(lev_e, 1)
            copies(7)
            dve.wait_ge(lev_exp, 8)
            V.tensor_tensor(qd[0][:, :, :], qkT[:, 0:2, :], ee[1][:, :, :], ALU.mult)
            V.tensor_tensor(kd[0][:, :, :], qkT[:, 2:4, :], ee[0][:, :, :], ALU.mult).then_inc(lev_qk, 1)
            for t in range(T - 1):
                dve.wait_ge(st_psum, t + 1)
                for h in range(LH):
                    f, p0 = h // 2, (h % 2) * 64
                    s_h = state[p0:p0 + 64, f, (h % 2) * P:(h % 2 + 1) * P]
                    new = ps[p0:p0 + 64, 4 + t, h * P:(h + 1) * P]
                    if t:
                        ins = V.scalar_tensor_tensor(out=s_h, in0=s_h, scalar=elast[p0:p0 + 64, f, t:t + 1], in1=new,
                                                     op0=ALU.mult, op1=ALU.add)
                    else:
                        ins = V.tensor_copy(s_h, new)
                ins.then_inc(st_ready, 1)
                dve.wait_ge(st_ready, t + 1)
            dve.wait_ge(act_gla, 5)
            own(V.tensor_reduce(ss[:, :], gsq[:, :, :].rearrange("p t (h d) -> p (t h) d", h=LH), AX.X, ALU.add))
            V.tensor_scalar(ss[:, :], ss[:, :], 1.0 / P, EPS, ALU.mult, ALU.add).then_inc(var_ready, 1)
            dve.wait_ge(std_ready, 2)
            own(V.reciprocal(rstd[:, :], rstd[:, :]))
            for t in range(T):
                o = proj[:, t, 512:1024].rearrange("p (h d) -> p h d", h=LH)
                own(V.tensor_tensor(o, ps[:, t, :].rearrange("p (h d) -> p h d", h=LH),
                                    rstd[:, 4 * t:4 * t + 4].unsqueeze(2).to_broadcast([P, LH, P]), ALU.mult))
                own(V.tensor_tensor(o, o, row[:, R_GLA:R_GLA + P].unsqueeze(1).to_broadcast([P, LH, P]), ALU.mult))
                ins = V.tensor_tensor(proj[:, t, 512:1024], proj[:, t, 512:1024], proj[:, t, 1024:1536], ALU.mult)
            ins.then_inc(dve_gla, 1)

            dve.wait_ge(pool_act, 8)
            V.memset(bd[:, :, :], 0.0)
            V.memset(xs[:, :, S:544], 0.0)
            own(V.memset(xs[64:128, :, S - 1:S], 0.0))
            for v in range(2):
                dve.wait_ge(c_saved, 4 * v + 4)
                for i in range(16):
                    if v:
                        dve.wait_ge(c_hid, 1)
                    src = xs[:, :, 2 * i:2 * i + 512].rearrange("p g (n s) -> p g n s", s=CST)[:, :, :, 0]
                    V.tensor_scalar(gt[:, i, :].rearrange("p (g n) -> p g n", g=G), src,
                                    vec[:, V_POS + 16 * v + i:V_POS + 16 * v + i + 1], None, ALU.add).then_inc(c_gt, 1)
                if v == 0:
                    dve.wait_ge(c_out, 1)
                    own(V.tensor_copy(kcn[:, 0, :], ps[:, 6, 0:DH]))
                    own(V.tensor_tensor(kcn[:, 1, :], kcn[:, 0, :], kcn[:, 0, :], ALU.mult))
                    own(V.tensor_reduce(ss[:, 0:1], kcn[:, 1, :], AX.X, ALU.add))
                    V.tensor_scalar(ss[:, 0:1], ss[:, 0:1], 1.0 / DH, EPS, ALU.mult, ALU.add).then_inc(var_ready, 1)
                    dve.wait_ge(std_ready, 3)
                    own(V.reciprocal(rstd[:, 0:1], rstd[:, 0:1]))
                    own(V.tensor_scalar(kcn[:, 0, :], kcn[:, 0, :], rstd[:, 0:1], None, ALU.mult))
                    own(V.tensor_tensor(kcn[:, 0, :], kcn[:, 0, :], row[:, R_KG:R_KG + DH], ALU.mult))
                    V.tensor_copy(kcn[:, 1, :], kcn[:, 0, :]).then_inc(c_dve, 1)

            dve.wait_ge(c_saved, 9)
            V.memset(mc[:, :], 0.0).then_inc(o_saved, 4)
            dve.wait_ge(o_saved, 4)
            units = [(t, r, b) for t in range(T) for r in range(R) for b in range(2)]
            per = 70
            with dve.Fori(0, G) as g:
                own.enter(g, per)
                dve.wait_ge(n_sq, g + 1)
                own(V.tensor_reduce(qss[:, :], sqs[:, :, :].rearrange("p t (h d) -> p (t h) d", d=DH), AX.X, ALU.add))
                V.tensor_scalar(qss[:, :], qss[:, :], 1.0 / DH, EPS, ALU.mult, ALU.add).then_inc(n_ssq, 1)
                dve.wait_ge(n_std, g + 1)
                own(V.reciprocal(qss[:, :], qss[:, :]))
                q3 = qss[:, :].rearrange("p (t h) -> p t h", t=T)
                own(V.tensor_scalar(q3[:, :, 0:R], q3[:, :, 0:R], -DH ** -0.5, None, ALU.mult))
                for t in range(T):
                    q_t = qn[:, t, :].rearrange("p (r d) -> p r d", r=R)
                    src = proj[:, t, bass.ds(1536 + g * 256, 256)].rearrange("p (r d) -> p r d", r=R)
                    own(V.tensor_tensor(q_t, src, q3[:, t, 0:R].unsqueeze(2).to_broadcast([P, R, DH]), ALU.mult))
                    own(V.tensor_tensor(q_t, q_t, row[:, R_QG:R_QG + DH].unsqueeze(1).to_broadcast([P, R, DH]),
                                        ALU.mult))
                    for b in range(2):
                        k_t = kn[:, b, t, :].rearrange("p (a d) -> p a d", a=2)
                        src = proj[:, t, bass.ds(3072 + 512 * b + g * DH, DH)]
                        own(V.tensor_scalar(k_t[:, 0, :], src, q3[:, t, R + b:R + b + 1], None, ALU.mult))
                        own(V.tensor_tensor(k_t[:, 0, :], k_t[:, 0, :], row[:, R_KG + DH * (b + 1):R_KG + DH * (b + 2)],
                                            ALU.mult))
                        last = V.tensor_copy(k_t[:, 1, :], k_t[:, 0, :])
                        if t == T - 1 and b == 1:
                            last.then_inc(n_qk, 1)
                        else:
                            own(last)
                dve.wait_ge(n_bias, g + 1)

                def cmp_soft(t):
                    dve.wait_ge(cs_psum, 4 * g + (t + 1))
                    if t:
                        dve.wait_ge(cp_ready, 4 * g + t)
                    own(V.tensor_tensor(sc[:, :], ps[:, 7, 0:R * NCMP], cmpb[:, t, bass.ds(g * R * NCMP, R * NCMP)],
                                        ALU.add))
                    s3 = sc[:, :].rearrange("p (r n) -> p r n", r=R)
                    own(V.tensor_reduce(mc[:, :], s3, AX.X, ALU.min))
                    own(V.tensor_scalar(mc[:, :], mc[:, :], 1e-6 * FAR, None, ALU.min))
                    V.tensor_tensor(s3, s3, mc[:, :].unsqueeze(2).to_broadcast([P, R, NCMP]),
                                    ALU.subtract).then_inc(cs_ready, 1)

                def cmp_sum(t):
                    dve.wait_ge(cp_ready, 4 * g + (t + 1))
                    own(V.tensor_reduce(den[:, t, :, 0], pc[:, :].rearrange("p (r n) -> p r n", r=R), AX.X, ALU.add))
                    own(V.tensor_scalar(den[:, t, :, 0], den[:, t, :, 0], 1e-30, None, ALU.max))

                def combine(t):
                    own(V.reciprocal(coef[:, t, :, :], den[:, t, :, :]))
                    gt_t = gN[:, t, bass.ds(16 + g * 12, 12)].rearrange("p (r b) -> p r b", b=3)
                    own(V.tensor_tensor(coef[:, t, :, :], coef[:, t, :, :], gt_t, ALU.mult))
                    dve.wait_ge(pv_done, 32 * g + 8 * (t + 1))
                    dve.wait_ge(cpv_done, 4 * g + (t + 1))
                    for b in range(3):
                        src = ps[:, 7, 256:512] if b == 0 else ps[:, 5 + t % 2, (b - 1) * 256:b * 256]
                        ins = V.tensor_tensor(oacc[:, b, :].rearrange("p (r d) -> p r d", r=R),
                                              src.rearrange("p (r d) -> p r d", r=R),
                                              coef[:, t, :, b:b + 1].to_broadcast([P, R, DH]), ALU.mult)
                    own(ins)
                    own(V.tensor_tensor(oacc[:, 0, :], oacc[:, 0, :], oacc[:, 1, :], ALU.add))
                    V.tensor_tensor(proj[:, t, bass.ds(1536 + g * 256, 256)], oacc[:, 0, :], oacc[:, 2, :],
                                    ALU.add).then_inc(o_saved, 1)
                    dve.wait_ge(o_saved, 4 * g + (t + 5))

                for n, (t, r, b) in enumerate(units):
                    w = (t + 1) * P
                    dve.wait_ge(s_psum, 32 * g + (n + 1))
                    if n >= 3:
                        dve.wait_ge(p_ready, 32 * g + (n - 2))
                    dve.sem_inc(dve_steps, 1)
                    V.tensor_tensor_reduce(out=sbuf[:, n % 3, 0:w], in0=ps[:, n % 3, 0:w], in1=biasT[:, r, S - w:S],
                                           scale=1.0, scalar=3e38, op0=ALU.add, op1=ALU.min,
                                           accum_out=mneg[:, n:n + 1]).then_inc(s_saved, 1)
                    if n % 8 == 6:
                        cmp_soft(t)
                    if n % 8 == 7:
                        cmp_sum(t)
                    if n % 8 == 2 and t:
                        combine(t - 1)
                dve.wait_ge(p_ready, 32 * g + 32)
                combine(T - 1)
            own.leave(G)

            for k in range(KD):
                dve.wait_ge(m_hi, k + 1)
                src = poolT[:, k, :] if k < 4 else ps[:, k % 8, :]
                V.tensor_tensor(mixL[:, k, :], src, mixH[:, k, :].bitcast(F32), ALU.subtract).then_inc(m_lo, 1)
            dve.wait_ge(m_lo, KD)
            V.memset(dtmp[:, 0, 0:1], 0.0).then_inc(x1_ready, 4)
            dve.wait_ge(x1_ready, 4)
            dve.wait_ge(x1_landed, 16 * T)
            with dve.Fori(0, 4) as i:
                own.enter(i, 4)
                for t in range(T):
                    if t < 3:
                        dve.wait_ge(tile_done, 3 * i + 27 + t + 1)
                    else:
                        dve.wait_ge(unit_used, 16 * i + used(U_OUT + KD))
                    col = bass.ds(512 * i, 512)
                    own(V.tensor_tensor(dtmp[:, t % 2, :], ps[:, t, :], grow[:, col], ALU.mult))
                    V.tensor_tensor(x1[:, t, col], x1[:, t, col], dtmp[:, t % 2, :], ALU.add).then_inc(x1_ready, 1)
                    dve.wait_ge(x1_ready, 4 * i + t + 5)
            own.leave(4)
            dve.wait_ge(f_sq, 1)
            V.tensor_scalar(ss[:, 4:8], ss[:, 0:4], 1.0 / D, EPS, ALU.mult, ALU.add).then_inc(f_var, 1)
            dve.wait_ge(f_std, 1)
            V.reciprocal(rstd[:, 0:4], rstd[:, 4:8]).then_inc(f_rstd, 1)
            for k in range(KD):
                dve.wait_ge(f_psum, k + 1)
                own(V.tensor_scalar(dtmp[:, k % 2, :], ps[:, k % 8, :], acol[:, k:k + 1], modc[:, 32 + k:33 + k],
                                    ALU.mult, ALU.add))
                own(V.tensor_copy(hfH[:, k, :], dtmp[:, k % 2, :]))
                V.tensor_tensor(hfL[:, k, :], dtmp[:, k % 2, :], hfH[:, k, :].bitcast(F32), ALU.subtract)\
                 .then_inc(f_ready, 1)
            dve.wait_ge(f_ready, KD)
            V.memset(hfull[:, 0, 0:1], 0.0).then_inc(up_saved, 2)
            V.memset(hfull[:, 0, 1:2], 0.0).then_inc(gate_saved, 2)
            V.memset(hfull[:, 0, 2:3], 0.0).then_inc(y_added, 4)
            dve.wait_ge(y_added, 4)
            with dve.Fori(0, FG) as i:
                own.enter(i, 16)
                for a in range(2):
                    for c in range(2):
                        n = 2 * a + c
                        if a and c == 0:
                            dve.wait_ge(h_lo, 4 * i + 2)
                        dve.wait_ge(gate_saved, 4 * i + n + 3)
                        if c == 0:
                            dve.wait_ge(tile_done, TD_FFN + 18 * i + 3 * a + 3)
                        else:
                            dve.wait_ge(unit_used, UNITS_FFN * i + used(U_FFN + KD * (a + 1)))
                        V.tensor_tensor(hfull[:, c, :], gsil[:, c, :], ps[:, 2 + c, :], ALU.mult).then_inc(up_saved, 1)
                        dve.wait_ge(up_saved, 4 * i + n + 3)
                    for c in range(2):
                        n = 2 * a + c
                        dve.wait_ge(h_hi, 4 * i + n + 1)
                        V.tensor_tensor(huL[:, n, :], hfull[:, c, :], huH[:, n, :].bitcast(F32),
                                        ALU.subtract).then_inc(h_lo, 1)
                for c in range(4):
                    for t in range(T):
                        if t < 3:
                            dve.wait_ge(tile_done, TD_FFN + 18 * i + 6 + 3 * c + t + 1)
                        else:
                            dve.wait_ge(unit_used, UNITS_FFN * i + used(U_FFN + 2 * KD + 4 * (c + 1)))
                        col = slice(512 * c, 512 * (c + 1))
                        own(V.tensor_tensor(dtmp[:, t % 2, :], ps[:, 4 + t, :], grow[:, D + 512 * c:D + 512 * (c + 1)],
                                            ALU.mult))
                        V.tensor_tensor(x1[:, t, col], x1[:, t, col], dtmp[:, t % 2, :], ALU.add).then_inc(y_added, 1)
                        dve.wait_ge(y_added, 16 * i + 4 * c + t + 5)
            own.leave(FG)


def shape_tables():
    i = np.arange(P)
    s_, t_ = i[:, None], i[None, :]
    bands = []
    for w in POOL_WINDOWS:
        inside = (s_ <= t_) & (s_ > t_ - w)
        own = (s_ == t_).astype(np.float32)
        bands += [inside / np.minimum(t_ + 1, w) - own, inside / w - own, (s_ - P > t_ - w) / w]
    masks = [s_ == t_]
    for h in LEVELS:
        masks.append((s_ // (2 * h) == t_ // (2 * h)) & (s_ % (2 * h) < h) & (t_ % (2 * h) >= h))
    away = s_ + (S - P) - np.arange(S)[None, :]
    away = np.where(away >= 0, away, FAR)
    tabs = np.concatenate([np.eye(P), np.ones((P, P))] + bands + masks + [away], axis=1).astype(np.float32)
    slopes = np.asarray([2.0 ** (-8.0 * (h + 1) / H) for h in range(H)], dtype=np.float32)
    n = np.arange(NCMP)
    gap = (np.arange(S)[:, None] - (n * CST + 31)[None, :]).astype(np.float32)
    bias = slopes[None, :, None] * gap[:, None, :]
    bias = np.where((gap >= 0)[:, None, :] & (n < NCMP - 1), bias, np.float32(FAR)).astype(np.float32)
    cmp_tab = bias.reshape(T, P, H * NCMP).transpose(1, 0, 2).reshape(P, T * H * NCMP)
    return tabs, slopes, np.ascontiguousarray(cmp_tab)


def lay_out(a):
    w_in, w_out, w_f, w_y = a["w_in"][0], a["w_out"][0], a["w_ffn_in"][0], a["w_ffn_out"][0]
    units = np.zeros((UNITS, P, U), np.float32)

    def k_tiles(w):
        return w.reshape(-1, P, w.shape[1])

    units[0:16] = k_tiles(w_in[:, 512:1024])
    narrow = k_tiles(np.concatenate([w_in[:, 2048:2064], w_in[:, 4624:4672]], axis=1))
    for k in range(KD):
        units[16 + k // 4, :, (k % 4) * 64:(k % 4) * 64 + 64] = narrow[k]
    n = 20
    for c in (0, 1024, 1536, 2064, 2576, 3088, 3600, 4112):
        units[n:n + KD] = k_tiles(w_in[:, c:c + U])
        n += KD
    for c in range(4):
        units[n:n + KD] = k_tiles(w_out[:, c * U:(c + 1) * U])
        n += KD
    for g in range(FG):
        for b in range(2):
            c = (2 * g + b) * 256
            units[n:n + KD, :, 0:256] = k_tiles(w_f[:, c:c + 256])
            units[n:n + KD, :, 256:512] = k_tiles(w_f[:, FFN + c:FFN + c + 256])
            n += KD
        for c in range(4):
            units[n:n + 4] = k_tiles(w_y[4 * P * g:4 * P * (g + 1), c * U:(c + 1) * U])
            n += 4
    stream = units.reshape(UNITS // 2, 2, P, U).transpose(0, 2, 1, 3).reshape(UNITS // 2 * P, 2 * U)
    order = (0, 1, 2, 5, 3, 4)
    w_mod = a["w_mod"][0].reshape(8, 2, P, 6, 4, U)[:, :, :, order]
    mstream = w_mod.transpose(3, 4, 0, 2, 1, 5).reshape(24 * 8 * P, 2 * U)
    b_mod = a["b_mod"][0].reshape(6, D)

    def cols(v):
        return v.reshape(-1, P).T

    tabs, slopes, cmp_tab = shape_tables()
    pos = a["nsa_cmp_pos"][0].reshape(2, 16, P).transpose(2, 0, 1).reshape(P, 32)
    vecs = np.concatenate([cols(a["c"][0]), cols(a["norm_mix_gain"][0]), cols(a["norm_ffn_gain"][0]),
                           cols(b_mod[0]), cols(b_mod[1]), cols(b_mod[3]), cols(b_mod[4]), cols(a["gla_b_gk"][0]),
                           cols(a["pool_scale"][0]), np.broadcast_to(slopes, (P, H)), pos], axis=1)
    rows = np.concatenate([a["nsa_q_gain"][0], a["nsa_k_gain"][0].reshape(-1), a["gla_norm_gain"][0]])
    return {
        "x": a["x"][0], "wstream": stream, "mstream": mstream, "vecs": vecs, "rows": rows,
        "grow_bias": np.concatenate([b_mod[2], b_mod[5]]), "tabs": tabs, "cmp_tab": cmp_tab,
        "up": a["gla_w_gk_up"][0], "pool_w": a["pool_w"][0].transpose(1, 0, 2).reshape(P, 4 * P),
        "w1": a["nsa_cmp_w1"][0].reshape(2, KD, P, 2 * P).transpose(0, 2, 1, 3).reshape(2, P, KD * 2 * P),
        "w2": a["nsa_cmp_w2"][0].reshape(2, 2, P, DH).transpose(2, 0, 1, 3).reshape(P, 4 * DH),
    }


def kernel(**inputs):
    import concourse.bacc as bacc
    from concourse.bass_utils import run_bass_kernel_spmd

    arrays = {n: np.ascontiguousarray(v) for n, v in lay_out({k: np.asarray(v) for k, v in inputs.items()}).items()}
    nc = bacc.Bacc("TRN2", target_bir_lowering=False, num_devices=1)
    args = {n: nc.dram_tensor("in_" + n, v.shape, mybir.dt.from_np(v.dtype), kind="ExternalInput").ap()
            for n, v in arrays.items()}
    y = nc.dram_tensor("out_y", (S, D), F32, kind="ExternalOutput").ap()
    layer_kernel(nc, out=y, **args)
    r = run_bass_kernel_spmd(nc, [{"in_" + n: v for n, v in arrays.items()}], core_ids=[0])
    return r.results[0]["out_y"].reshape(1, S, D)
```
